# Optimizing a Trainium2 kernel written in Bass

```python
import jax, jax.numpy as jnp
from jax import lax
import numpy as np

D_MODEL = 1024
BATCH = 1
SEQ = 256
DEPTH = 2

N_A_LAYERS = DEPTH // 2
N_B_LAYERS = DEPTH - N_A_LAYERS
D_RNN = D_MODEL
LRU_BLOCKS = 4
LRU_BLOCK_W = D_RNN // LRU_BLOCKS
CONV_W = 4
LRU_C = 8.0
N_HEADS = 8
HEAD_DIM = D_MODEL // N_HEADS
ROT_DIM = HEAD_DIM // 4
ROPE_THETA = 500000.0
MOBA_BLOCK = 256
MOBA_TOPK = 3
Q_CHUNK = 64
N_EXPERTS = 64
N_GROUPS = 8
TOPK_GROUPS = 4
TOPK_EXPERTS = 8
D_EXPERT = 256
D_SHARED = 256
ROUTED_SCALE = 2.5
MOE_ROW_BLOCK = 256
PLE_DIM = 256
DN_ALPHA = (2 * DEPTH) ** 0.25
DN_BETA = (8 * DEPTH) ** -0.25
LN_EPS = 1e-5

kernel_name = 'yoco_rglru_moba_moe_deepnorm'

def layer_norm(x, g, b):
    xf = x.astype(jnp.float32)
    mu = xf.mean(-1, keepdims=True)
    var = jnp.square(xf - mu).mean(-1, keepdims=True)
    y = (xf - mu) * lax.rsqrt(var + LN_EPS) * g.astype(jnp.float32) + b.astype(jnp.float32)
    return y.astype(x.dtype)

def rope_tables(seq, dtype):
    inv = ROPE_THETA ** (-jnp.arange(0, ROT_DIM, 2, dtype=jnp.float32) / ROT_DIM)
    ang = jnp.arange(seq, dtype=jnp.float32)[:, None] * inv[None, :]
    return jnp.cos(ang).astype(dtype), jnp.sin(ang).astype(dtype)

def apply_partial_rope(t, cos, sin):
    c = cos[None, :, None, :]
    s = sin[None, :, None, :]
    half = ROT_DIM // 2
    x1 = t[..., :half]
    x2 = t[..., half:ROT_DIM]
    return jnp.concatenate([x1 * c - x2 * s, x2 * c + x1 * s, t[..., ROT_DIM:]], axis=-1)

def _lin_combine(c1, c2):
    a1, b1 = c1
    a2, b2 = c2
    return a1 * a2, a2 * b1 + b2

def rglru_block(x, w_in, b_in, conv_w, conv_b, ga_w, ga_b, gi_w, gi_b, lam, w_out):
    B, S, _ = x.shape
    xy = x @ w_in + b_in
    xb, yb = jnp.split(xy, 2, axis=-1)
    y = jax.nn.gelu(yb, approximate=True)
    xp = jnp.pad(xb, ((0, 0), (CONV_W - 1, 0), (0, 0)))
    xc = conv_b + sum(xp[:, k:k + S] * conv_w[k] for k in range(CONV_W))
    xg = xc.reshape(B, S, LRU_BLOCKS, LRU_BLOCK_W)
    r = jax.nn.sigmoid(jnp.einsum('bsnc,ncd->bsnd', xg, ga_w) + ga_b).reshape(B, S, D_RNN)
    i = jax.nn.sigmoid(jnp.einsum('bsnc,ncd->bsnd', xg, gi_w) + gi_b).reshape(B, S, D_RNN)
    log_a = (-LRU_C * r.astype(jnp.float32)) * jax.nn.softplus(-lam.astype(jnp.float32))
    a = jnp.exp(log_a)
    u = jnp.sqrt(-jnp.expm1(2.0 * log_a)) * (i * xc).astype(jnp.float32)
    _, h = lax.associative_scan(_lin_combine, (a, u), axis=1)
    return (h.astype(x.dtype) * y) @ w_out

def shared_kv(xs, g, b, w_kv, cos, sin):
    B, S, _ = xs.shape
    h = layer_norm(xs, g, b)
    kv = (h @ w_kv).reshape(B, S, 2, N_HEADS, HEAD_DIM)
    k = apply_partial_rope(kv[:, :, 0], cos, sin).transpose(0, 2, 1, 3)
    v = kv[:, :, 1].transpose(0, 2, 1, 3)
    nb = -(-S // MOBA_BLOCK)
    pad = nb * MOBA_BLOCK - S
    k_blk = jnp.pad(k, ((0, 0), (0, 0), (0, pad), (0, 0))).reshape(B, N_HEADS, nb, MOBA_BLOCK, HEAD_DIM)
    v_blk = jnp.pad(v, ((0, 0), (0, 0), (0, pad), (0, 0))).reshape(B, N_HEADS, nb, MOBA_BLOCK, HEAD_DIM)
    k_mean = k_blk.astype(jnp.float32).mean(axis=3)
    return k_blk, v_blk, k_mean

def moba_attention(x, w_q, w_o, k_blk, v_blk, k_mean, cos, sin):
    B, S, _ = x.shape
    nb = k_blk.shape[2]
    tk = min(MOBA_TOPK, nb)
    q = apply_partial_rope((x @ w_q).reshape(B, S, N_HEADS, HEAD_DIM), cos, sin) * (HEAD_DIM ** -0.5)
    q = q.transpose(0, 2, 1, 3)
    bi = jnp.arange(B)[:, None, None, None]
    hi = jnp.arange(N_HEADS)[None, :, None, None]
    blk_ids = jnp.arange(nb)

    def chunk(c):
        q0 = c * Q_CHUNK
        qc = lax.dynamic_slice_in_dim(q, q0, Q_CHUNK, axis=2)
        own = q0 // MOBA_BLOCK
        gate = jnp.einsum('bhqd,bhnd->bhqn', qc.astype(jnp.float32), k_mean)
        gate = jnp.where(blk_ids < own, gate, -jnp.inf)
        _, sel = lax.top_k(gate, tk)
        valid = sel < own
        k_sel = k_blk[bi, hi, sel]
        v_sel = v_blk[bi, hi, sel]
        s_sel = jnp.einsum('bhqd,bhqjkd->bhqjk', qc, k_sel, preferred_element_type=jnp.float32)
        s_sel = jnp.where(valid[..., None], s_sel, -jnp.inf).reshape(B, N_HEADS, Q_CHUNK, tk * MOBA_BLOCK)
        k_own = lax.dynamic_index_in_dim(k_blk, own, axis=2, keepdims=False)
        v_own = lax.dynamic_index_in_dim(v_blk, own, axis=2, keepdims=False)
        s_own = jnp.einsum('bhqd,bhkd->bhqk', qc, k_own, preferred_element_type=jnp.float32)
        qpos = q0 + jnp.arange(Q_CHUNK)
        kpos = own * MOBA_BLOCK + jnp.arange(MOBA_BLOCK)
        s_own = jnp.where(kpos[None, :] <= qpos[:, None], s_own, -jnp.inf)
        probs = jax.nn.softmax(jnp.concatenate([s_sel, s_own], axis=-1), axis=-1).astype(v_blk.dtype)
        p_sel = probs[..., :tk * MOBA_BLOCK].reshape(B, N_HEADS, Q_CHUNK, tk, MOBA_BLOCK)
        p_own = probs[..., tk * MOBA_BLOCK:]
        return (jnp.einsum('bhqjk,bhqjkd->bhqd', p_sel, v_sel)
                + jnp.einsum('bhqk,bhkd->bhqd', p_own, v_own))

    out = lax.map(chunk, jnp.arange(S // Q_CHUNK))
    out = out.transpose(1, 0, 3, 2, 4).reshape(B, S, N_HEADS * HEAD_DIM)
    return out @ w_o

def moe_ffn(x, router_w, router_b, w_gate, w_up, w_down, s_gate, s_up, s_down):
    B, S, D = x.shape
    N = B * S
    M = MOE_ROW_BLOCK
    xt = x.reshape(N, D)
    scores = jax.nn.sigmoid(jnp.einsum('nd,de->ne', xt, router_w, preferred_element_type=jnp.float32))
    choice = scores + router_b.astype(jnp.float32)
    grp = choice.reshape(N, N_GROUPS, N_EXPERTS // N_GROUPS)
    grp_score = lax.top_k(grp, 2)[0].sum(-1)
    _, grp_idx = lax.top_k(grp_score, TOPK_GROUPS)
    grp_mask = jax.nn.one_hot(grp_idx, N_GROUPS, dtype=jnp.float32).sum(1) > 0
    expert_mask = jnp.repeat(grp_mask, N_EXPERTS // N_GROUPS, axis=1)
    choice = jnp.where(expert_mask, choice, -jnp.inf)
    _, e_idx = lax.top_k(choice, TOPK_EXPERTS)
    w = jnp.take_along_axis(scores, e_idx, axis=1)
    w = w / w.sum(-1, keepdims=True) * ROUTED_SCALE
    NK = N * TOPK_EXPERTS
    flat_e = e_idx.reshape(NK)
    flat_tok = jnp.repeat(jnp.arange(N, dtype=jnp.int32), TOPK_EXPERTS)
    flat_w = w.reshape(NK)
    order = jnp.argsort(flat_e)
    se, stok, sw = flat_e[order], flat_tok[order], flat_w[order]
    counts = jnp.bincount(flat_e, length=N_EXPERTS)
    starts = jnp.cumsum(counts) - counts
    padded = (counts + M - 1) // M * M
    pends = jnp.cumsum(padded)
    pstarts = pends - padded
    pos = pstarts[se] + jnp.arange(NK) - starts[se]
    n_blocks = -(-NK // M) + N_EXPERTS
    R = n_blocks * M
    buf_tok = jnp.zeros((R,), jnp.int32).at[pos].set(stok)
    buf_w = jnp.zeros((R,), jnp.float32).at[pos].set(sw)
    blk_e = jnp.minimum(jnp.searchsorted(pends, jnp.arange(n_blocks) * M, side='right'), N_EXPERTS - 1)

    def step(acc, blk):
        tok, wt, e = blk
        xs = xt[tok]
        hdn = jax.nn.silu(xs @ w_gate[e]) * (xs @ w_up[e])
        y = (hdn @ w_down[e]).astype(jnp.float32) * wt[:, None]
        return acc.at[tok].add(y), None

    acc, _ = lax.scan(step, jnp.zeros((N, D), jnp.float32),
                      (buf_tok.reshape(n_blocks, M), buf_w.reshape(n_blocks, M), blk_e))
    shared = (jax.nn.silu(xt @ s_gate) * (xt @ s_up)) @ s_down
    return (acc.astype(x.dtype) + shared).reshape(B, S, D)

def setup_inputs(seed: int = 0) -> dict:
    key = jax.random.key(seed)
    ks = iter(jax.random.split(key, 32))
    f32 = jnp.float32

    def nrm(shape, scale):
        return jax.random.normal(next(ks), shape, f32) * scale

    x = nrm((BATCH, SEQ, D_MODEL), 1.0)
    p = nrm((DEPTH, BATCH, SEQ, PLE_DIM), 1.0)
    ln_g = 1.0 + nrm((DEPTH, 2, D_MODEL), 0.02)
    ln_b = nrm((DEPTH, 2, D_MODEL), 0.02)
    a_w_in = nrm((N_A_LAYERS, D_MODEL, 2 * D_RNN), D_MODEL ** -0.5)
    a_b_in = nrm((N_A_LAYERS, 2 * D_RNN), 0.01)
    a_conv_w = nrm((N_A_LAYERS, CONV_W, D_RNN), CONV_W ** -0.5)
    a_conv_b = nrm((N_A_LAYERS, D_RNN), 0.01)
    a_gate_a_w = nrm((N_A_LAYERS, LRU_BLOCKS, LRU_BLOCK_W, LRU_BLOCK_W), LRU_BLOCK_W ** -0.5)
    a_gate_a_b = nrm((N_A_LAYERS, LRU_BLOCKS, LRU_BLOCK_W), 0.01)
    a_gate_i_w = nrm((N_A_LAYERS, LRU_BLOCKS, LRU_BLOCK_W, LRU_BLOCK_W), LRU_BLOCK_W ** -0.5)
    a_gate_i_b = nrm((N_A_LAYERS, LRU_BLOCKS, LRU_BLOCK_W), 0.01)
    u = jax.random.uniform(next(ks), (N_A_LAYERS, D_RNN), f32, minval=0.9, maxval=0.999)
    s = u ** (1.0 / LRU_C)
    a_lambda = jnp.log(s) - jnp.log1p(-s)
    a_w_out = nrm((N_A_LAYERS, D_RNN, D_MODEL), D_RNN ** -0.5 * DN_BETA)
    kv_ln_g = 1.0 + nrm((D_MODEL,), 0.02)
    kv_ln_b = nrm((D_MODEL,), 0.02)
    w_kv = nrm((D_MODEL, 2 * N_HEADS * HEAD_DIM), D_MODEL ** -0.5)
    b_w_q = nrm((N_B_LAYERS, D_MODEL, N_HEADS * HEAD_DIM), D_MODEL ** -0.5)
    b_w_o = nrm((N_B_LAYERS, N_HEADS * HEAD_DIM, D_MODEL), (N_HEADS * HEAD_DIM) ** -0.5 * DN_BETA)
    router_w = nrm((DEPTH, D_MODEL, N_EXPERTS), D_MODEL ** -0.5)
    router_b = nrm((DEPTH, N_EXPERTS), 0.01)
    exp_w_gate = nrm((DEPTH, N_EXPERTS, D_MODEL, D_EXPERT), D_MODEL ** -0.5)
    exp_w_up = nrm((DEPTH, N_EXPERTS, D_MODEL, D_EXPERT), D_MODEL ** -0.5)
    exp_w_down = nrm((DEPTH, N_EXPERTS, D_EXPERT, D_MODEL), D_EXPERT ** -0.5 * DN_BETA)
    sh_w_gate = nrm((DEPTH, D_MODEL, D_SHARED), D_MODEL ** -0.5)
    sh_w_up = nrm((DEPTH, D_MODEL, D_SHARED), D_MODEL ** -0.5)
    sh_w_down = nrm((DEPTH, D_SHARED, D_MODEL), D_SHARED ** -0.5 * DN_BETA)
    ple_w = nrm((DEPTH, PLE_DIM, D_MODEL), PLE_DIM ** -0.5)
    ple_gate_w = nrm((DEPTH, D_MODEL, D_MODEL), D_MODEL ** -0.5)
    return {'x': x, 'p': p, 'ln_g': ln_g, 'ln_b': ln_b,
            'a_w_in': a_w_in, 'a_b_in': a_b_in, 'a_conv_w': a_conv_w, 'a_conv_b': a_conv_b,
            'a_gate_a_w': a_gate_a_w, 'a_gate_a_b': a_gate_a_b, 'a_gate_i_w': a_gate_i_w,
            'a_gate_i_b': a_gate_i_b, 'a_lambda': a_lambda, 'a_w_out': a_w_out,
            'kv_ln_g': kv_ln_g, 'kv_ln_b': kv_ln_b, 'w_kv': w_kv, 'b_w_q': b_w_q, 'b_w_o': b_w_o,
            'router_w': router_w, 'router_b': router_b, 'exp_w_gate': exp_w_gate,
            'exp_w_up': exp_w_up, 'exp_w_down': exp_w_down, 'sh_w_gate': sh_w_gate,
            'sh_w_up': sh_w_up, 'sh_w_down': sh_w_down, 'ple_w': ple_w, 'ple_gate_w': ple_gate_w}

def reference(x, p, ln_g, ln_b, a_w_in, a_b_in, a_conv_w, a_conv_b, a_gate_a_w, a_gate_a_b,
              a_gate_i_w, a_gate_i_b, a_lambda, a_w_out, kv_ln_g, kv_ln_b, w_kv, b_w_q, b_w_o,
              router_w, router_b, exp_w_gate, exp_w_up, exp_w_down, sh_w_gate, sh_w_up,
              sh_w_down, ple_w, ple_gate_w):
    S = x.shape[1]
    cos, sin = rope_tables(S, x.dtype)
    for i in range(DEPTH):
        if i < N_A_LAYERS:
            mix = rglru_block(x, a_w_in[i], a_b_in[i], a_conv_w[i], a_conv_b[i], a_gate_a_w[i],
                              a_gate_a_b[i], a_gate_i_w[i], a_gate_i_b[i], a_lambda[i], a_w_out[i])
        else:
            if i == N_A_LAYERS:
                k_blk, v_blk, k_mean = shared_kv(x, kv_ln_g, kv_ln_b, w_kv, cos, sin)
            j = i - N_A_LAYERS
            mix = moba_attention(x, b_w_q[j], b_w_o[j], k_blk, v_blk, k_mean, cos, sin)
        x = layer_norm(DN_ALPHA * x + mix, ln_g[i, 0], ln_b[i, 0])
        ffn = moe_ffn(x, router_w[i], router_b[i], exp_w_gate[i], exp_w_up[i], exp_w_down[i],
                      sh_w_gate[i], sh_w_up[i], sh_w_down[i])
        x = layer_norm(DN_ALPHA * x + ffn, ln_g[i, 1], ln_b[i, 1])
        x = x + (p[i] @ ple_w[i]) * jax.nn.sigmoid(x @ ple_gate_w[i])
    return x


_drawn_inputs = setup_inputs


def setup_inputs(seed=0):
    import zlib

    import numpy as np

    out = dict(_drawn_inputs(seed))
    spreads = {}
    factors = {'a_gate_a_b': 8.0, 'a_gate_i_b': 8.0, 'kv_ln_g': 6.702, 'kv_ln_b': 3.555}
    for name, (base, spread) in spreads.items():
        noise = np.random.default_rng([zlib.crc32(name.encode()), seed]).standard_normal(out[name].shape)
        drawn = base * np.exp(spread * noise) if base else spread * noise
        out[name] = __import__('jax').numpy.asarray(drawn.astype(out[name].dtype))
    for name, factor in factors.items():
        out[name] = (out[name] * factor).astype(out[name].dtype)
    return out
```

```python
from contextlib import ExitStack

import numpy as np

import concourse.bass as bass
from concourse import mybir

F32 = mybir.dt.float32
F32R = mybir.dt.float32r
BF16 = mybir.dt.bfloat16
I32 = mybir.dt.int32
ALU = mybir.AluOpType
ACT = mybir.ActivationFunctionType
AX_X = mybir.AxisListType.X

P = 128
D = 1024
KC = D // P
T = 256
TC = T // P
HALF = 512
NH, DH = 8, 128
ROT = DH // 4
HR = ROT // 2
NE, NG, EPG = 64, 8, 8
TOPG, TOPE = 4, 8
DE = 256
FC = DE // P
ROUTED_SCALE = 2.5
PLE = 256
LAYERS = 2
ALPHA = float((2 * LAYERS) ** 0.25)
LN_EPS = 1e-5
KV_NORM = 2
LRU_C = 8.0
SCALE = float(DH) ** -0.5

CAP = 64
NJ = T // CAP
OVER = 32
NCOL = NJ * NE + 1
NOBLK = NJ * NE
TABLE = NE + OVER + 8
NITER_MIN = NE // 4
NITER_MAX = (NE + OVER) // 4
AWAY = 1000.0

UNIT = 2048
NUNITS = 18
EXPERT = 3 * UNIT
GU = KC * 2 * DE

C_ID, C_IOTA, C_ROPE = 0, P, P + CAP
C_QM = C_ROPE + TC * 2 * ROT
C_LT = C_QM + (NJ - 1) * NE
C_KK = C_LT + NG * NG
C_S1 = C_KK + 8
C_N = C_S1 + 1
V_BIN, V_CW, V_CB, V_GA, V_GI, V_LAM, V_KG, V_KB, V_N = 0, 16, 48, 56, 64, 72, 80, 88, 96


def build(nc, xt_d, x_d, pt_d, cst_d, cstb_d, chan_d, rows_d, tab_d, win_d, gates_d, wout_d, shared_d,
          router_d, experts_d, ple_d, pgate_d, wkv_d, wq_d, wo_d, out_d):
    ctx = ExitStack()
    with ctx:
        def sb(name, shape, dt=F32):
            return ctx.enter_context(nc.sbuf_tensor(name, shape, dt))

        def sem(name):
            return ctx.enter_context(nc.semaphore(name))

        base = -(-nc.sbuf_base // 32) * 32
        z = sb("z", [P, TC, D])
        lnp = sb("lnp", [P, 2, D])
        R = sb("scratch", [P, 3, KC, T])
        z_at, lnp_at, scratch_at = (base + i * TC * D * 4 for i in range(3))

        def split(name, shape, offset):
            return nc.alloc_sbuf_tensor_at(name, shape, F32R, offset=offset)

        W = sb("weights", [P, NUNITS, UNIT])
        x_res = sb("x_res", [P, TC, D])
        xT = sb("xT", [P, KC, T])
        R2 = sb("scratch2", [P, 12 * P + 8 * ROT])
        ptk = sb("ple_in", [P, 2, T])
        cst = sb("cst", [P, C_N])
        chan = sb("chan", [P, V_N])
        rb = sb("router_bias", [P, LAYERS, NE])
        bconst = sb("bconst", [P, 4, P], BF16)
        ident_b, upper_b, ones_b, causal_b = (bconst[:, i, :] for i in range(4))
        stats = sb("stats", [P, TC, 2, 6])
        mv = sb("mv", [P, TC, 2])
        lnv = sb("lnv", [P, TC, 4])
        eps = sb("eps", [P, 1])
        lam = sb("lam", [P, 6, KC])
        tab = sb("tab", [1, LAYERS, 2, TABLE], I32)
        pads = R2[:, 0:4 * (T + 3)].rearrange("p (b t) -> p b t", b=4)
        xc, th, ig = R[:, 0], R[:, 1], R[:, 2]
        yv = z[:, :, :].rearrange("p c (k t) -> p (c k) t", t=T)
        sq = lnp[:, :, :].rearrange("p c (k t) -> p (c k) t", t=T)
        flat = R[:, :, :, :].rearrange("p a k t -> p (a k t)")
        at = [0]

        def cut(n):
            at[0] += n
            assert at[0] <= 3 * KC * T
            return flat[:, at[0] - n:at[0]]

        def cut_split(name, shape):
            n = int(np.prod(shape[1:]))
            at[0] += n
            return split(name, shape, scratch_at + (at[0] - n) * 4)
        x_hi = split("x_hi", [P, TC, D], lnp_at)
        x_lo = split("x_lo", [P, TC, D], z_at)
        xg = cut(KC * 2 * P).rearrange("p (k s) -> p k s", k=KC)
        oh = cut_split("onehot", [P, TC, 2 * P])
        ohw = cut(TC * P).rearrange("p (c s) -> p c s", c=TC)
        sg = cut(DE)
        hh = cut(DE)
        hT = cut(DE).rearrange("p (f s) -> p f s", f=FC)
        ohT = cut_split("onehot_T", [P, T])
        y_hi = cut_split("y_hi", [P, D])
        y_lo = cut_split("y_lo", [P, D])
        wslot = sb("slot_weight", [P, 1])
        routw = flat[:, 4 * D:5 * D].rearrange("p (k e) -> p k e", k=KC)
        rt = flat[:, 5 * D:6 * D].rearrange("p (a c e) -> p a c e", a=8, c=TC)
        shT = R2[:, D:D + TC * DE].rearrange("p (f c s) -> p f c s", f=FC, c=TC)
        rankt = sb("rankt", [P, TC, NCOL])
        wgtt = sb("wgtt", [P, TC, NCOL])
        score, choice, cm, mrep, selm, w8 = (rt[:, i] for i in range(6))
        cmp2 = rt[:, 6:8]
        gtmp = sb("gtmp", [P, TC, 3, NG])
        m8 = R2[:, 0:TC * NE].rearrange("p (c g e) -> p c g e", c=TC, g=NG)
        top8 = sb("top8", [P, TC, 8])
        wsum = sb("wsum", [P, TC, 2])
        selb = sb("selb", [P, TC, NE], BF16)
        ovr = R2[:, TC * NE:TC * NE + 3 * (NJ - 1) * NE].rearrange("p (a n) -> p a n", a=3)
        ovs = sb("over_s", [P, 4])
        onesr = sb("ones_row", [P, (NJ - 1) * NE])
        kT, vt, hkT = R[:, 0], R[:, 1].rearrange("p k t -> p (k t)").rearrange("p (c n) -> p c n", c=TC), R[:, 2]
        qT = R[:, 2]
        oT = xT
        tokm = z
        ropet = R2[:, 12 * P:12 * P + 8 * ROT].rearrange("p (a h d) -> p a h d", a=2, h=4)
        prob = R2[:, 0:6 * P].rearrange("p (b n) -> p b n", b=2)
        prT = R2[:, 6 * P:12 * P].rearrange("p (b n) -> p b n", b=2)
        mxs = sb("mxs", [P, NH, TC, 4])

        PS = ctx.enter_context(nc.psum_tensor("ps", [P, 8, HALF], F32))
        ident = cst[:, C_ID:C_ID + P]
        iota = cst[:, C_IOTA:C_IOTA + CAP]

        small = sem("small_loaded")
        xt_in = sem("xT_loaded")
        x_in = sem("x_loaded")
        zero_ok = sem("pads_zeroed")
        unit_sem = [sem(f"unit{u}_loaded") for u in range(NUNITS)]
        chain = sem("dve_step")
        achain = sem("act_step")
        gchain = sem("pool_step")
        out_s = sem("out_stored")
        names = {}

        def S(name):
            if name not in names:
                names[name] = sem(name)
            return names[name]

        loaded_at, loads_of = {}, [0] * NUNITS

        def planned(name, u):
            loads_of[u] += 16
            loaded_at[name] = (u, loads_of[u])
            return u

        def E(s):
            return W[:, 3 * s:3 * s + 3, :].rearrange("p a n -> p (a n)")

        X0 = 12
        for i in range(4):
            planned(f"win{i}", i)
        planned("gates0", 4), planned("gates1", 5)
        for i in range(4, 8):
            planned(f"win{i}", X0 + i - 4)
        planned("sh0_0", 16), planned("sh1_0", 17)
        for i in range(4):
            planned(f"wout{i}", 6 + i)
        planned("sh2_0", 12)
        for i in range(4):
            planned(f"pg{i}_0", 13 + i)
        planned("ple_0", 17)
        planned("wk0", 12)
        for i in range(1, 4):
            planned(f"wk{i}", i - 1)
        for i in range(4):
            planned(f"wv{i}", 3 + i)
        for i in range(4):
            planned(f"wq{i}", 7 + i)
        planned("wo0", 11)
        for i in range(1, 4):
            planned(f"wo{i}", 12 + i)
        planned("sh0_1", 16), planned("sh1_1", 17), planned("sh2_1", 12)
        for i in range(4):
            planned(f"pg{i}_1", 13 + i)
        planned("ple_1", 17)

        def unit(name):
            return W[:, loaded_at[name][0], :]

        def kmajor(name):
            return unit(name).rearrange("p (k n) -> p k n", k=2)

        def arrived(eng, name):
            u, n = loaded_at[name]
            eng.wait_ge(unit_sem[u], n)

        def link(eng, s, counter, ins):
            counter[0] += 1
            ins.then_inc(s, 1)
            eng.wait_ge(s, counter[0])

        block = ctx.enter_context(nc.Block())

        @block.sync
        def _(sp):
            def load(name, src):
                sp.dma_start(unit(name), src).then_inc(unit_sem[loaded_at[name][0]], 16)

            def expert(L, s, e):
                sp.dma_start(E(s)[:, 0:GU], experts_d[L, e, :, 0:GU]).then_inc(S(f"gu{s // 2}_loaded_{L}"), 16)
                sp.dma_start(E(s)[:, GU:EXPERT], experts_d[L, e, :, GU:EXPERT]).then_inc(S(f"down{s // 2}_loaded_{L}"), 16)

            sp.dma_start(chan[:, :], chan_d).then_inc(small, 16)
            sp.dma_start(xT[:, :, :], xt_d).then_inc(xt_in, 16)
            for i in range(4):
                load(f"win{i}", win_d[i])
            sp.dma_start(cst[:, :], cst_d).then_inc(small, 16)
            sp.dma_start(bconst[:, :, :], cstb_d).then_inc(small, 16)
            load("gates0", gates_d[0])
            load("gates1", gates_d[1])
            for i in range(4, 8):
                load(f"win{i}", win_d[i])
            for i in range(4):
                load(f"wout{i}", wout_d[i])
            load("sh0_0", shared_d[0, 0])
            load("sh1_0", shared_d[0, 1])
            sp.wait_ge(S("xb_mm"), KC)
            expert(0, 0, 0)
            sp.wait_ge(S("gate_mm"), KC)
            expert(0, 1, 1)
            for i, u in enumerate(("sh2_0", "pg0_0", "pg1_0", "pg2_0")):
                sp.wait_ge(S("yb_mm"), 2 * i + 2)
                load(u, shared_d[0, 2] if i == 0 else pgate_d[0, i - 1])
            sp.wait_ge(S("mix_mm"), TC * 2)
            expert(0, 2, 2)
            expert(0, 3, 3)

            def expert_loop(L):
                sp.wait_ge(S("table"), 1 * L + 1)
                n = sp.value_load(tab[0:1, L, 0, TABLE - 1:TABLE], min_val=NITER_MIN, max_val=NITER_MAX)
                with sp.Fori(1, n) as i:
                    for b in range(2):
                        es = [sp.value_load(tab[0:1, L, 1, bass.ds(i * 4 + 2 * b + s, 1)], min_val=0, max_val=NE - 1)
                              for s in range(2)]
                        sp.wait_ge(S(f"gu_mm_{L}"), i * 2 + (b - 1))
                        for s in range(2):
                            sp.dma_start(E(2 * b + s)[:, 0:GU],
                                         experts_d[L, bass.ds(es[s], 1), :, 0:GU].rearrange("a p n -> (a p) n")
                                         ).then_inc(S(f"gu{b}_loaded_{L}"), 16)
                        sp.wait_ge(S(f"down_mm_{L}"), i * 4 + (2 * b - 2))
                        for s in range(2):
                            sp.dma_start(E(2 * b + s)[:, GU:EXPERT],
                                         experts_d[L, bass.ds(es[s], 1), :, GU:EXPERT].rearrange("a p n -> (a p) n")
                                         ).then_inc(S(f"down{b}_loaded_{L}"), 16)
                last = sp.value_load(tab[0:1, L, 0, TABLE - 2:TABLE - 1], min_val=NITER_MIN - 1, max_val=NITER_MAX - 1)
                return n, last

            sp.wait_ge(S("shared_gu_mm"), TC)
            load("pg3_0", pgate_d[0, 3])
            load("ple_0", ple_d[0])
            sp.wait_ge(S("shared_down_mm"), 1)
            load("wk0", wkv_d[0, 0])
            n, last = expert_loop(0)
            sp.wait_ge(S("down_mm_0"), last * 4 + 2)
            for i in range(1, 4):
                load(f"wk{i}", wkv_d[0, i])
            for i in range(3):
                load(f"wv{i}", wkv_d[1, i])
            sp.wait_ge(S("down_mm_0"), n * 4)
            load("wv3", wkv_d[1, 3])
            for i in range(4):
                load(f"wq{i}", wq_d[i])
            load("wo0", wo_d[0])
            sp.wait_ge(S("pgate_mm"), TC * 2)
            for i in range(1, 4):
                load(f"wo{i}", wo_d[i])
            load("sh0_1", shared_d[1, 0])
            load("sh1_1", shared_d[1, 1])
            sp.wait_ge(S("k_mm"), TC * 2)
            load("sh2_1", shared_d[1, 2])
            expert(1, 0, 0)
            sp.wait_ge(S("v_mm"), TC * 2)
            expert(1, 1, 1)
            sp.wait_ge(S("q_mm"), TC * 2)
            expert(1, 2, 2)
            sp.wait_ge(S("mix_mm"), 4 + TC * 2)
            expert(1, 3, 3)
            for i in range(3):
                load(f"pg{i}_1", pgate_d[1, i])
            sp.wait_ge(S("shared_gu_mm"), 2 + TC)
            load("pg3_1", pgate_d[1, 3])
            load("ple_1", ple_d[1])
            expert_loop(1)
            for c in range(TC):
                for h in range(2):
                    sp.wait_ge(S("x_out"), 4 + 2 * c + h + 1)
                    sp.dma_start(out_d[0, P * c:P * c + P, HALF * h:HALF * h + HALF],
                                 x_res[:, c, HALF * h:HALF * h + HALF]).then_inc(out_s, 16)
            sp.wait_ge(out_s, 16 * TC * 2)

        @block.tensor
        def _(pe):
            def mm(out, lhsT, rhs, first, last, shared_bank=False):
                return nc.tensor.matmul(out, lhsT, rhs, start=first, stop=last, skip_group_check=shared_bank)

            def bank(b, n=HALF):
                return PS[:, b, 0:n]

            pe.wait_ge(xt_in, 16)
            for b in range(KC):
                if b % 2 == 0:
                    arrived(pe, f"win{b // 2}")
                if b >= 4:
                    pe.wait_ge(S("xb_out"), b - 3)
                w = unit(f"win{b // 2}").rearrange("p (b k c) -> p b k c", b=2, k=KC)
                for k in range(KC):
                    m = mm(bank(4 + b % 4, T), w[:, b % 2, k, :], xT[:, k, :], k == 0, k == KC - 1)
                m.then_inc(S("xb_mm"), 1)

            def gates(b):
                if b == 0:
                    arrived(pe, "gates0")
                    arrived(pe, "gates1")
                if b >= 4:
                    pe.wait_ge(S("gate_out"), 2 * (b - 3))
                pe.wait_ge(S("conv"), 2 * (b // 2) + 2)
                n, dc = b // 2, b % 2
                for g in range(2):
                    w = unit(f"gates{g}").rearrange("p (n c d) -> p n c d", n=4, c=2)
                    for cc in range(2):
                        m = mm(PS[:, b % 4, g * T:g * T + T], w[:, n, cc, dc * P:dc * P + P],
                               xc[:, 2 * n + cc, :], cc == 0, cc == 1)
                m.then_inc(S("gate_mm"), 1)

            def y_block(b):
                if b % 2 == 0:
                    arrived(pe, f"win{4 + b // 2}")
                if b < 4:
                    pe.wait_ge(S("xb_out"), KC - 3 + b)
                else:
                    pe.wait_ge(S("gelu"), b - 3)
                w = unit(f"win{4 + b // 2}").rearrange("p (b k c) -> p b k c", b=2, k=KC)
                for k in range(KC):
                    m = mm(bank(4 + b % 4, T), w[:, b % 2, k, :], xT[:, k, :], k == 0, k == KC - 1)
                m.then_inc(S("yb_mm"), 1)

            for b in range(6):
                gates(b)
            y_block(0)
            gates(6)
            gates(7)
            for b in range(1, KC):
                y_block(b)
            pe.wait_ge(S("gate_out"), 2 * KC)
            for i in range(4):
                arrived(pe, f"wout{i}")
            pe.wait_ge(S("hy"), 1)
            for c in range(TC):
                for h in range(2):
                    for k in range(KC):
                        m = mm(bank(2 * c + h), yv[:, k, c * P:c * P + P],
                               kmajor(f"wout{k // 2}")[:, k % 2, h * HALF:h * HALF + HALF], k == 0, k == KC - 1)
                    m.then_inc(S("mix_mm"), 1)

            def transposes(src):
                for q in range(4):
                    for kk in range(2):
                        for c in range(TC):
                            k = 2 * q + kk
                            m = nc.tensor.transpose(PS[:, 4 + q, (2 * kk + c) * P:(2 * kk + c + 1) * P],
                                                    src[:, c, k * P:k * P + P], ident)
                    m.then_inc(S("xT_mm"), 1)

            def moe(L):
                pe.wait_ge(S("x1_out"), 4 * L + 2 * TC)
                transposes(x_res)
                for q in range(4):
                    pe.wait_ge(S("xT_out"), 4 * 3 * L + q + 1)
                pe.wait_ge(S("router_loaded"), 16 * (L + 1))
                for c in range(TC):
                    for k in range(KC):
                        m = mm(PS[:, 4, c * P:c * P + P], xT[:, k, c * P:c * P + P], routw[:, k, :], k == 0, k == KC - 1)
                m.then_inc(S("logit_mm"), 1)
                arrived(pe, f"sh0_{L}")
                arrived(pe, f"sh1_{L}")
                for c in range(TC):
                    for k in range(KC):
                        u = unit(f"sh{k // 4}_{L}").rearrange("p (k n) -> p k n", k=4)
                        m = mm(bank(5 + c), xT[:, k, c * P:c * P + P], u[:, k % 4, :], k == 0, k == KC - 1)
                    m.then_inc(S("shared_gu_mm"), 1)
                pe.wait_ge(S("picked"), 1 * L + 1)
                for c in range(TC):
                    for cc in range(c + 1):
                        mm(PS[:, 7, c * NE:c * NE + NE], upper_b if cc == c else ones_b, selb[:, cc, :],
                           cc == 0, cc == c)
                for cc in range(TC):
                    m = mm(PS[:, 7, TC * NE:TC * NE + NE], ones_b, selb[:, cc, :], cc == 0, cc == TC - 1)
                m.then_inc(S("rank_mm"), 1)
                pe.wait_ge(S("scored"), 1 * L + 1)
                for c in range(TC):
                    pe.wait_ge(S("shared_h"), 2 * L + c + 1)
                    for f in range(FC):
                        m = nc.tensor.transpose(PS[:, 4, (f * TC + c) * P:(f * TC + c + 1) * P],
                                                (sg, hh)[c][:, f * P:f * P + P], ident)
                    m.then_inc(S("shared_t_mm"), 1)
                pe.wait_ge(S("shared_t_out"), 1 * L + 1)
                arrived(pe, f"sh2_{L}")
                for c in range(TC):
                    for h in range(2):
                        for f in range(FC):
                            m = mm(bank(2 * c + h), shT[:, f, c, :],
                                   kmajor(f"sh2_{L}")[:, f, h * HALF:h * HALF + HALF], f == 0, False, True)
                m.then_inc(S("shared_down_mm"), 1)
                pe.wait_ge(S("over"), 1 * L + 1)
                mm(PS[0:1, 7, 256:256 + OVER], ovs[0:OVER, 0:1], ident[0:OVER, 0:OVER], True, True
                   ).then_inc(S("over_mm"), 1)

                def gather(q, bank_no):
                    for kk in range(2):
                        k = 2 * q + kk
                        for j, part in enumerate((x_hi, x_lo)):
                            for c in range(TC):
                                m = mm(PS[:, bank_no, kk * 2 * P:(kk + 1) * 2 * P], part[:, c, k * P:k * P + P],
                                       oh[:, c, :], j == 0 and c == 0, j == 1 and c == TC - 1)
                    m.then_inc(S(f"gather_mm_{L}"), 1)

                def scatter(last):
                    for c in range(TC):
                        for j, part in enumerate((y_hi, y_lo)):
                            for h in range(2):
                                m = mm(bank(2 * c + h), ohT[:, c * P:c * P + P], part[:, h * HALF:h * HALF + HALF],
                                       False, last and j == 1, True)
                    m.then_inc(S(f"scatter_mm_{L}"), 1)

                pe.wait_ge(S("x_split"), 2 * L + 2)
                pe.wait_ge(S(f"onehot_{L}"), 1)
                pe.wait_ge(S("table"), L + 1)
                for q in range(4):
                    gather(q, 4 + q)
                pe.sem_inc(S(f"turn_mm_{L}"), 1)
                n = pe.value_load(tab[0:1, L, 0, TABLE - 1:TABLE], min_val=NITER_MIN, max_val=NITER_MAX)
                with pe.Fori(0, n) as i:
                    for b in range(2):
                        g = i * 2 + b
                        pe.wait_ge(S(f"gu{b}_loaded_{L}"), i * 32 + 32)
                        if b == 0:
                            pe.wait_ge(S(f"gathered_{L}"), i * 4 + 4)
                        pe.wait_ge(S(f"hidden_{L}"), g + 1)
                        for k in range(KC):
                            for s in range(2):
                                m = mm(PS[s * CAP:s * CAP + CAP, 6, :], xg[:, k, b * P + s * CAP:b * P + s * CAP + CAP],
                                       E(2 * b + s)[:, k * 2 * DE:(k + 1) * 2 * DE], k == 0, k == KC - 1, True)
                        m.then_inc(S(f"gu_mm_{L}"), 1)
                        pe.wait_ge(S(f"y_out_{L}"), g * 2 + 2)
                        if b == 1:
                            pe.wait_ge(S(f"onehot_{L}"), i + 2)
                            gather(0, 4)
                            gather(1, 5)
                        pe.wait_ge(S(f"turned_{L}"), g + 1)
                        scatter(False)
                        if b == 1:
                            for q in (2, 3):
                                pe.wait_ge(S(f"gathered_{L}"), i * 4 + (3 + q))
                                gather(q, 2 + q)
                        pe.wait_ge(S(f"hidden_{L}"), g + 2)
                        for f in range(FC):
                            nc.tensor.transpose(PS[:, 7, f * P:f * P + P], hh[:, f * P:f * P + P], ident)
                        for c in range(TC):
                            m = nc.tensor.transpose(PS[:, 7, (2 + c) * P:(3 + c) * P], ohw[:, c, :], ident)
                        m.then_inc(S(f"turn_mm_{L}"), 1)
                        pe.wait_ge(S(f"down{b}_loaded_{L}"), i * 32 + 32)
                        pe.wait_ge(S(f"hidT_{L}"), g + 1)
                        if b == 1:
                            pe.wait_ge(S(f"gathered_{L}"), i * 4 + 8)
                        for h in range(2):
                            for f in range(FC):
                                for s in range(2):
                                    m = mm(PS[s * CAP:s * CAP + CAP, 4 + h, :], hT[:, f, s * CAP:s * CAP + CAP],
                                           E(2 * b + s)[:, GU + f * D + h * HALF:GU + f * D + h * HALF + HALF],
                                           f == 0, f == FC - 1, True)
                            m.then_inc(S(f"down_mm_{L}"), 1)
                pe.wait_ge(S(f"y_out_{L}"), n * 4 + 2)
                pe.wait_ge(S(f"turned_{L}"), n * 2 + 1)
                scatter(True)

            def ple(L):
                arrived(pe, f"ple_{L}")
                if L:
                    pe.wait_ge(S("ple_in_1"), 16)
                pe.wait_ge(S("moe_read"), 1 * L + 1)
                for t in range(TC * 2):
                    c, h = t // 2, t % 2
                    for k in range(2):
                        m = mm(bank(t), ptk[:, k, c * P:c * P + P],
                               kmajor(f"ple_{L}")[:, k, h * HALF:h * HALF + HALF], k == 0, k == 1)
                m.then_inc(S("ple_mm"), 1)
                pe.wait_ge(S("x2_out"), 4 * L + 2 * TC)
                transposes(x_res)
                for q in range(4):
                    pe.wait_ge(S("xT_out"), 4 * (3 * L + 1) + q + 1)
                    arrived(pe, f"pg{q}_{L}")
                for t in range(TC * 2):
                    c, h = t // 2, t % 2
                    for k in range(KC):
                        m = mm(bank(4 + t), xT[:, k, c * P:c * P + P],
                               kmajor(f"pg{k // 2}_{L}")[:, k % 2, h * HALF:h * HALF + HALF], k == 0, k == KC - 1)
                    m.then_inc(S("pgate_mm"), 1)

            moe(0)
            ple(0)

            pe.wait_ge(S("x_out"), TC * 2)
            transposes(x_res)
            pe.wait_ge(S("norm_z"), TC * (KV_NORM + 1))
            for q in range(4):
                for kk in range(2):
                    for c in range(TC):
                        k = 2 * q + kk
                        m = nc.tensor.transpose(PS[:, q, (2 * kk + c) * P:(2 * kk + c + 1) * P],
                                                z[:, c, k * P:k * P + P], ident)
                m.then_inc(S("hT_mm"), 1)
            for k in range(KC):
                pe.wait_ge(S("hT_out"), k + 1)

            def project(lhs, name, done, banks_free):
                for i in range(4):
                    arrived(pe, f"{name}{i}")
                for t in range(TC * 2):
                    c, h = t // 2, t % 2
                    if banks_free:
                        pe.wait_ge(S(banks_free), t + 1)
                    for k in range(KC):
                        m = mm(bank(4 + t), lhs[:, k, c * P:c * P + P],
                               kmajor(f"{name}{k // 2}")[:, k % 2, h * HALF:h * HALF + HALF], k == 0, k == KC - 1)
                    m.then_inc(S(done), 1)

            def head_transposes():
                for q in range(4):
                    for kk in range(2):
                        for c in range(TC):
                            m = nc.tensor.transpose(PS[:, q, (2 * kk + c) * P:(2 * kk + c + 1) * P],
                                                    tokm[:, c, (2 * q + kk) * P:(2 * q + kk + 1) * P], ident)
                    m.then_inc(S("heads_mm"), 1)

            for q in range(4):
                pe.wait_ge(S("xT_out"), 4 * 2 + q + 1)
            project(hkT, "wk", "k_mm", None)
            project(hkT, "wv", "v_mm", "k_rope")
            head_transposes()
            project(xT, "wq", "q_mm", "v_out")
            pe.wait_ge(S("q_rope"), 4)
            for q in range(4):
                pe.wait_ge(S("heads_out"), q + 1)
            head_transposes()
            for q in range(4):
                pe.wait_ge(S("heads_out"), 4 + q + 1)

            def head_scores(h):
                b = 4 + h % 2
                if h >= 2:
                    pe.wait_ge(S("exped"), h - 1)
                mm(PS[:, b, 0:P], qT[:, h, 0:P], kT[:, h, 0:P], True, False, True)
                mm(PS[:, b, 0:P], ident_b, causal_b, False, True, True)
                mm(PS[:, b, P:3 * P], qT[:, h, P:T], kT[:, h, :], True, False, True)
                mm(PS[:, b, 2 * P:3 * P], ident_b, causal_b, False, True, True).then_inc(S("score_mm"), 1)

            def head_turn(h):
                b = 6 + h % 2
                pe.wait_ge(S("probs"), h + 1)
                if h >= 2:
                    pe.wait_ge(S("probT_out"), h - 1)
                for j in range(3):
                    m = nc.tensor.transpose(PS[:, b, j * P:j * P + P], prob[:, h % 2, j * P:j * P + P], ident)
                m.then_inc(S("probT_mm"), 1)

            def head_values(h):
                b, o = (h // 2) % 2, (h % 2) * T
                pe.wait_ge(S("probT_out"), h + 1)
                if h >= 4 and h % 2 == 0:
                    pe.wait_ge(S("oT_out"), h // 2 - 1)
                mm(PS[:, b, o:o + T], vt[:, 0, h * P:h * P + P], prT[:, h % 2, 0:T], True, False, True)
                mm(PS[:, b, o + P:o + T], vt[:, 1, h * P:h * P + P], prT[:, h % 2, T:3 * P], False, True, True
                   ).then_inc(S("value_mm"), 1)

            for i in range(NH + 2):
                if i < NH:
                    head_scores(i)
                if 1 <= i <= NH:
                    head_turn(i - 1)
                if i >= 2:
                    head_values(i - 2)
            for i in range(4):
                arrived(pe, f"wo{i}")
            pe.wait_ge(S("oT_out"), NH // 2)
            for c in range(TC):
                for h in range(2):
                    for k in range(KC):
                        m = mm(bank(2 * c + h), oT[:, k, c * P:c * P + P],
                               kmajor(f"wo{k // 2}")[:, k % 2, h * HALF:h * HALF + HALF], k == 0, k == KC - 1)
                    m.then_inc(S("mix_mm"), 1)
            moe(1)
            ple(1)

        @block.scalar
        def _(act):
            def a(out, in_, f, **kw):
                return nc.scalar.activation(out, in_, f, **kw)

            act.dma_start(rb[:, :, :], rows_d[8 * D:8 * D + LAYERS * NE].rearrange("(a l e) -> a l e", a=1, l=LAYERS)
                          .broadcast_to([P, LAYERS, NE])).then_inc(small, 16)
            act.dma_start(tab[0:1], tab_d).then_inc(small, 16)
            act.dma_start(ptk[:, :, :], pt_d[:, 0]).then_inc(small, 16)
            act.dma_start(x_res[:, :, :], x_d).then_inc(x_in, 16)

            def load_norm(n):
                act.dma_start(lnp[:, :, :], rows_d[2 * n * D:2 * (n + 1) * D].rearrange("(a l e) -> a l e", a=1, l=2)
                              .broadcast_to([P, 2, D])).then_inc(S("norm_loaded"), 16)

            act.wait_ge(small, 16 * 6)
            act.wait_ge(zero_ok, 1)
            a(lam[:, 0, :], chan[:, V_LAM:V_LAM + KC], ACT.Abs).then_inc(S("lam_abs"), 1)
            act.wait_ge(S("lam_abs"), 1)
            a(lam[:, 1, :], lam[:, 0, :], ACT.Exp, scale=-1.0).then_inc(S("lam_exp"), 1)
            for b in range(KC):
                act.wait_ge(S("xb_mm"), b + 1)
                if b >= 4:
                    act.wait_ge(S("conv"), b - 3)
                a(pads[:, b % 4, 3:T + 3], PS[:, 4 + b % 4, 0:T], ACT.Identity,
                  bias=chan[:, V_BIN + b:V_BIN + b + 1]).then_inc(S("xb_out"), 1)
            for b in range(KC):
                act.wait_ge(S("gate_mm"), b + 1)
                a(th[:, b, :], PS[:, b % 4, 0:T], ACT.Sigmoid, bias=chan[:, V_GA + b:V_GA + b + 1]
                  ).then_inc(S("gate_out"), 1)
                a(ig[:, b, :], PS[:, b % 4, T:2 * T], ACT.Sigmoid, bias=chan[:, V_GI + b:V_GI + b + 1]
                  ).then_inc(S("gate_out"), 1)
                act.wait_ge(S("gate_out"), 2 * b + 1)
                act.wait_ge(S("lam_ready"), 1)
                a(th[:, b, :], th[:, b, :], ACT.Tanh, scale=lam[:, 5, b:b + 1]).then_inc(S("tanh"), 1)
            act.wait_ge(S("tanh"), KC)
            for j in range(2):
                a(sq[:, 4 * j:4 * j + 4, :], th[:, 4 * j:4 * j + 4, :], ACT.Sqrt).then_inc(S("sqrt"), 1)
            for b in range(KC):
                act.wait_ge(S("yb_mm"), b + 1)
                a(yv[:, b, :], PS[:, 4 + b % 4, 0:T], ACT.Gelu_apprx_tanh,
                  bias=chan[:, V_BIN + 8 + b:V_BIN + 9 + b]).then_inc(S("gelu"), 1)
            act.wait_ge(S("hy"), 1)
            load_norm(0)
            act.dma_start(routw, router_d).then_inc(S("router_loaded"), 16)

            def norm(q):
                for c in range(TC):
                    act.wait_ge(S("norm_var"), TC * q + c + 1)
                    a(lnv[:, c, 0:1], mv[:, c, 1:2], ACT.Sqrt, bias=eps[:, 0:1]).then_inc(S("norm_sd"), 1)
                    act.wait_ge(S("norm_rstd"), TC * q + c + 1)
                    a(z[:, c, :], (x_res if q == KV_NORM else z)[:, c, :], ACT.Identity, scale=lnv[:, c, 1:2],
                      bias=lnv[:, c, 2:3]).then_inc(S("norm_z"), 1)

            def even_banks(dst, name, n, first_bank=4):
                for q in (0, 2):
                    act.wait_ge(S(f"{name}_mm"), 4 * n + q + 1)
                    if q:
                        act.wait_ge(S(f"{name}_out"), 4 * n + q)
                    a(dst[:, 2 * q:2 * q + 2, :].rearrange("p k t -> p (k t)"), PS[:, first_bank + q, :], ACT.Copy
                      ).then_inc(S(f"{name}_out"), 1)

            def moe(L):
                norm(3 * L)
                even_banks(xT, "xT", 3 * L)
                act.wait_ge(S("x1_out"), 4 * L + 2 * TC)
                a(x_hi[:, :, :], x_res[:, :, :], ACT.Copy).then_inc(S("x_split"), 1)
                act.wait_ge(S("logit_mm"), 1 * L + 1)
                a(score, PS[:, 4, 0:2 * P].rearrange("p (c n) -> p c n", c=TC)[:, :, L * NE:L * NE + NE], ACT.Sigmoid
                  ).then_inc(S("scored"), 1)
                for c in range(TC):
                    act.wait_ge(S("shared_gu_mm"), 2 * L + c + 1)
                    a((sg, hh)[c], PS[:, 5 + c, 0:DE], ACT.Silu).then_inc(S("shared_silu"), 1)

                def gathered(q, bank_no):
                    a(xg[:, 2 * q:2 * q + 2, :].rearrange("p k s -> p (k s)"), PS[:, bank_no, :], ACT.Copy
                      ).then_inc(S(f"gathered_{L}"), 1)

                act.wait_ge(S("table"), 1 * L + 1)
                n = act.value_load(tab[0:1, L, 0, TABLE - 1:TABLE], min_val=NITER_MIN, max_val=NITER_MAX)
                for q in range(4):
                    act.wait_ge(S(f"gather_mm_{L}"), q + 1)
                    gathered(q, 4 + q)
                with act.Fori(0, n) as i:
                    for b in range(2):
                        g = i * 2 + b
                        act.wait_ge(S(f"gu_mm_{L}"), g + 1)
                        act.wait_ge(S(f"hidden_{L}"), g + 1)
                        a(sg, PS[:, 6, 0:DE], ACT.Silu).then_inc(S(f"silu_{L}"), 1)
                        if b == 1:
                            for q in range(4):
                                act.wait_ge(S(f"gather_mm_{L}"), i * 4 + (5 + q))
                                gathered(q, 4 + q % 2)
                        act.wait_ge(S(f"turned_{L}"), g + 2)
                        for h in range(2):
                            act.wait_ge(S(f"down_mm_{L}"), g * 2 + h + 1)
                            a(y_hi[:, h * HALF:h * HALF + HALF], PS[:, 4 + h, :], ACT.Copy, scale=wslot[:, 0:1]
                              ).then_inc(S(f"y_hi_{L}"), 1)
                load_norm(2 * L + 1)

            def ple(L):
                norm(3 * L + 1)
                even_banks(xT, "xT", 3 * L + 1)
                if L == 0:
                    load_norm(2)
                    act.wait_ge(S("ple_mm"), 1)
                    act.dma_start(ptk[:, :, :], pt_d[:, 1]).then_inc(S("ple_in_1"), 16)
                for t in range(TC * 2):
                    act.wait_ge(S("pgate_mm"), 4 * L + t + 1)
                    a(z[:, t // 2, (t % 2) * HALF:(t % 2) * HALF + HALF], PS[:, 4 + t, :], ACT.Sigmoid
                      ).then_inc(S("pgate"), 1)

            moe(0)
            ple(0)

            norm(KV_NORM)
            even_banks(xT, "xT", 2)
            for k in range(KC):
                act.wait_ge(S("hT_mm"), k // 2 + 1)
                a(hkT[:, k, :], PS[:, k // 2, (k % 2) * T:(k % 2) * T + T], ACT.Identity,
                  scale=chan[:, V_KG + k:V_KG + k + 1], bias=chan[:, V_KB + k:V_KB + k + 1]).then_inc(S("hT_out"), 1)

            def copy_heads(done, mm_done):
                for t in range(TC * 2):
                    act.wait_ge(S(mm_done), t + 1)
                    a(tokm[:, t // 2, (t % 2) * HALF:(t % 2) * HALF + HALF], PS[:, 4 + t, :], ACT.Copy
                      ).then_inc(S(done), 1)

            act.wait_ge(S("hT_mm"), 4)
            copy_heads("k_copied", "k_mm")
            for t in range(TC * 2):
                act.wait_ge(S("v_mm"), t + 1)
                a(vt[:, t // 2, (t % 2) * HALF:(t % 2) * HALF + HALF], PS[:, 4 + t, :], ACT.Copy
                  ).then_inc(S("v_out"), 1)
            even_banks(kT, "heads", 0, 0)
            act.wait_ge(S("heads_mm"), 4)
            copy_heads("q_copied", "q_mm")
            even_banks(qT, "heads", 1, 0)

            def turned(h):
                act.wait_ge(S("probT_mm"), h + 1)
                if h >= 2:
                    act.wait_ge(S("value_mm"), h - 1)
                a(prT[:, h % 2, :], PS[:, 6 + h % 2, 0:3 * P], ACT.Copy).then_inc(S("probT_out"), 1)

            def heads_done(j):
                act.wait_ge(S("value_mm"), 2 * j + 2)
                a(oT[:, 2 * j:2 * j + 2, :].rearrange("p k t -> p (k t)"), PS[:, j % 2, :], ACT.Copy
                  ).then_inc(S("oT_out"), 1)

            for i in range(NH + 3):
                if i < NH:
                    act.wait_ge(S("negmax"), i + 1)
                    if i >= 2:
                        act.wait_ge(S("probT_mm"), i - 1)
                    a(prob[:, i % 2, 0:P], PS[:, 4 + i % 2, 0:P], ACT.Exp, scale=SCALE,
                      bias=mxs[:, i, 0, 1:2], accum_out=mxs[:, i, 0, 2:3])
                    a(prob[:, i % 2, P:3 * P], PS[:, 4 + i % 2, P:3 * P], ACT.Exp, scale=SCALE,
                      bias=mxs[:, i, 1, 1:2], accum_out=mxs[:, i, 1, 2:3]).then_inc(S("exped"), 1)
                if 1 <= i <= NH:
                    turned(i - 1)
                if i >= 3 and i % 2 == 1:
                    heads_done((i - 3) // 2)
            act.dma_start(routw, router_d).then_inc(S("router_loaded"), 16)
            moe(1)
            ple(1)

        @block.gpsimd
        def _(pool):
            nc.gpsimd.memset(pads[:, :, 0:3], 0.0).then_inc(S("pads0"), 1)
            nc.gpsimd.memset(eps[:, :], LN_EPS).then_inc(S("pads0"), 1)
            nc.gpsimd.memset(onesr[:, :], 1.0).then_inc(S("pads0"), 1)
            nc.gpsimd.memset(rankt[:, :, NOBLK:NCOL], -AWAY).then_inc(S("pads0"), 1)
            nc.gpsimd.memset(wgtt[:, :, NOBLK:NCOL], 0.0).then_inc(S("pads0"), 1)
            pool.wait_ge(S("pads0"), 5)
            nc.gpsimd.memset(ovs[:, 2:4], 0.0).then_inc(zero_ok, 1)

            def moe(L):
                pool.wait_ge(S("x_split"), 2 * L + 1)
                nc.gpsimd.tensor_tensor(x_lo[:, :, :], x_res[:, :, :], x_hi[:, :, :].bitcast(F32), ALU.subtract
                                        ).then_inc(S("x_split"), 1)
                pool.wait_ge(S("table"), L + 1)
                for part in (y_hi, y_lo):
                    nc.gpsimd.memset(part[:, :].bitcast(F32), 0.0).then_inc(S(f"y_out_{L}"), 1)
                nc.gpsimd.memset(ohT[:, :].bitcast(F32), 0.0).then_inc(S(f"turned_{L}"), 1)
            moe(0)
            moe(1)

        @block.vector
        def _(dve):
            count = [0]

            def step(ins):
                link(dve, chain, count, ins)

            v = nc.vector
            dve.wait_ge(small, 16 * 6)
            dve.wait_ge(zero_ok, 1)
            dve.wait_ge(S("lam_exp"), 1)
            step(v.tensor_scalar(lam[:, 2, :], lam[:, 1, :], 2.0, None, ALU.add))
            step(v.reciprocal(lam[:, 2, :], lam[:, 2, :]))
            step(v.tensor_tensor(lam[:, 2, :], lam[:, 2, :], lam[:, 1, :], ALU.mult))
            step(v.tensor_tensor(lam[:, 3, :], lam[:, 2, :], lam[:, 2, :], ALU.mult))
            step(v.tensor_scalar(lam[:, 4, :], lam[:, 3, :], 1.0 / 17, 1.0 / 15, ALU.mult, ALU.add))
            for m in (13, 11, 9, 7, 5, 3, 1):
                step(v.tensor_tensor(lam[:, 4, :], lam[:, 4, :], lam[:, 3, :], ALU.mult))
                step(v.tensor_scalar(lam[:, 4, :], lam[:, 4, :], 1.0 / m, None, ALU.add))
            step(v.scalar_tensor_tensor(lam[:, 4, :], lam[:, 4, :], 2.0, lam[:, 2, :], ALU.mult, ALU.mult))
            step(v.tensor_scalar(lam[:, 3, :], chan[:, V_LAM:V_LAM + KC], -1.0, 0.0, ALU.mult, ALU.max))
            step(v.tensor_tensor(lam[:, 4, :], lam[:, 4, :], lam[:, 3, :], ALU.add))
            v.tensor_scalar(lam[:, 5, :], lam[:, 4, :], LRU_C / 2, None, ALU.mult).then_inc(S("lam_ready"), 1)
            for b in range(KC):
                dve.wait_ge(S("xb_out"), b + 1)
                x4 = pads[:, b % 4, :]
                step(v.tensor_scalar(xc[:, b, :], x4[:, 0:T], chan[:, V_CW + b:V_CW + b + 1],
                                     chan[:, V_CB + b:V_CB + b + 1], ALU.mult, ALU.add))
                for k in range(1, 4):
                    w = chan[:, V_CW + 8 * k + b:V_CW + 8 * k + b + 1]
                    ins = v.scalar_tensor_tensor(xc[:, b, :], x4[:, k:k + T], w, xc[:, b, :], ALU.mult, ALU.add)
                    if k < 3:
                        step(ins)
                    else:
                        ins.then_inc(S("conv"), 1)
            for j in range(2):
                js = slice(4 * j, 4 * j + 4)
                dve.wait_ge(S("gate_out"), 8 * j + 8)
                step(v.tensor_tensor(ig[:, js, :], ig[:, js, :], xc[:, js, :], ALU.mult))
                dve.wait_ge(S("sqrt"), j + 1)
                if j == 0:
                    dve.wait_ge(S("gate_mm"), KC)
                step(v.tensor_scalar(th[:, js, :], th[:, js, :], 1.0, None, ALU.add))
                step(v.reciprocal(xc[:, js, :], th[:, js, :]))
                step(v.tensor_scalar(th[:, js, :], xc[:, js, :], 2.0, -1.0, ALU.mult, ALU.add))
                step(v.scalar_tensor_tensor(sq[:, js, :], xc[:, js, :], 2.0, sq[:, js, :], ALU.mult, ALU.mult))
                step(v.tensor_tensor(sq[:, js, :], sq[:, js, :], ig[:, js, :], ALU.mult))
                for b in range(4 * j, 4 * j + 4):
                    ins = v.tensor_tensor_scan(xc[:, b, :], th[:, b, :], sq[:, b, :], 0.0, ALU.mult, ALU.add)
                step(ins)
            for j in range(2):
                js = slice(4 * j, 4 * j + 4)
                dve.wait_ge(S("gelu"), 4 * j + 4)
                ins = v.tensor_tensor(yv[:, js, :], yv[:, js, :], xc[:, js, :], ALU.mult)
            ins.then_inc(S("hy"), 1)

            def norm_stats(c, src):
                for h in range(2):
                    ins = v.bn_stats(stats[:, c, h, :], src[:, c, h * HALF:h * HALF + HALF])
                step(ins)
                v.bn_aggr(mv[:, c, :], stats[:, c, :, :].rearrange("p a b -> p (a b)")).then_inc(S("norm_var"), 1)

            def norm_scale(q, c):
                dve.wait_ge(S("norm_sd"), TC * q + c + 1)
                step(v.reciprocal(lnv[:, c, 1:2], lnv[:, c, 0:1]))
                v.scalar_tensor_tensor(lnv[:, c, 2:3], mv[:, c, 0:1], -1.0, lnv[:, c, 1:2], ALU.mult, ALU.mult
                                       ).then_inc(S("norm_rstd"), 1)

            def norm_gain(q, n, out):
                dve.wait_ge(S("norm_loaded"), 16 * (n + 1))
                for c in range(TC):
                    dve.wait_ge(S("norm_z"), TC * q + c + 1)
                    for h in range(2):
                        hs = slice(h * HALF, h * HALF + HALF)
                        v.tensor_tensor(x_res[:, c, hs], z[:, c, hs], lnp[:, 0, hs], ALU.mult).then_inc(chain, 1)
                        count[0] += 1
                    for h in range(2):
                        hs = slice(h * HALF, h * HALF + HALF)
                        dve.wait_ge(chain, count[0] - 1 + h)
                        v.tensor_tensor(x_res[:, c, hs], x_res[:, c, hs], lnp[:, 1, hs], ALU.add).then_inc(S(out), 1)

            def residual(c, h):
                hs = slice(h * HALF, h * HALF + HALF)
                return v.scalar_tensor_tensor(z[:, c, hs], x_res[:, c, hs], ALPHA, PS[:, 2 * c + h, :], ALU.mult, ALU.add)

            def norm1(L):
                for c in range(TC):
                    for h in range(2):
                        dve.wait_ge(S("mix_mm"), 4 * L + 2 * c + h + 1 if L else 4)
                        ins = residual(c, h)
                    step(ins)
                    norm_stats(c, z)
                for c in range(TC):
                    norm_scale(3 * L, c)
                norm_gain(3 * L, 2 * L, "x1_out")

            def odd_banks(dst, name, n, first_bank=4):
                for q in (1, 3):
                    dve.wait_ge(S(f"{name}_mm"), 4 * n + q + 1)
                    dve.wait_ge(S(f"{name}_out"), 4 * n + q)
                    v.tensor_copy(dst[:, 2 * q:2 * q + 2, :].rearrange("p k t -> p (k t)"), PS[:, first_bank + q, :]
                                  ).then_inc(S(f"{name}_out"), 1)

            def moe(L):
                norm1(L)
                odd_banks(xT, "xT", 3 * L)
                dve.wait_ge(S("scored"), 1 * L + 1)
                step(v.tensor_tensor(choice, score, rb[:, L, :].unsqueeze(1).broadcast_to([P, TC, NE]), ALU.add))
                for c in range(TC):
                    for g in range(NG):
                        ins = v.max(m8[:, c, g, :], choice[:, c, g * EPG:g * EPG + EPG])
                step(ins)
                gs, gr, gm = gtmp[:, :, 0, :], gtmp[:, :, 1, :], gtmp[:, :, 2, :]
                step(v.tensor_tensor(gs, m8[:, :, :, 0], m8[:, :, :, 1], ALU.add))
                for c in range(TC):
                    mine = gs[:, c, :].unsqueeze(2).broadcast_to([P, NG, NG])
                    other = gs[:, c, :].unsqueeze(1).broadcast_to([P, NG, NG])
                    v.tensor_tensor(cmp2[:, 0, c, :].rearrange("p (a b) -> p a b", a=NG), other, mine, ALU.is_gt)
                    ins = v.tensor_tensor(cmp2[:, 1, c, :].rearrange("p (a b) -> p a b", a=NG), other, mine, ALU.is_equal)
                step(ins)
                step(v.tensor_tensor(cmp2[:, 1], cmp2[:, 1], cst[:, C_LT:C_LT + NE].unsqueeze(1).broadcast_to([P, TC, NE]),
                                     ALU.mult))
                step(v.tensor_tensor(cmp2[:, 0], cmp2[:, 0], cmp2[:, 1], ALU.add))
                for c in range(TC):
                    ins = v.tensor_reduce(gr[:, c, :], cmp2[:, 0, c, :].rearrange("p (a b) -> p a b", a=NG), AX_X, ALU.add)
                step(ins)
                step(v.tensor_scalar(gm, gr, TOPG - 0.5, -1e30, ALU.is_gt, ALU.mult))
                for c in range(TC):
                    ins = v.tensor_tensor(cm[:, c, :].rearrange("p (a b) -> p a b", a=NG),
                                          choice[:, c, :].rearrange("p (a b) -> p a b", a=NG),
                                          gm[:, c, :].unsqueeze(2).broadcast_to([P, NG, EPG]), ALU.add)
                step(ins)
                for c in range(TC):
                    ins = v.max(top8[:, c, :], cm[:, c, :])
                step(ins)
                for c in range(TC):
                    ins = v.match_replace(mrep[:, c, :], top8[:, c, :], cm[:, c, :], -3e38)
                step(ins)
                step(v.tensor_tensor(selm, mrep, cm, ALU.not_equal))
                v.tensor_copy(selb[:, :, :], selm).then_inc(S("picked"), 1)
                step(v.tensor_tensor(w8, selm, score, ALU.mult))
                step(v.tensor_reduce(wsum[:, :, 0:1].rearrange("p c o -> p (c o)"), w8, AX_X, ALU.add))
                step(v.reciprocal(wsum[:, :, 1], wsum[:, :, 0]))
                for c in range(TC):
                    ins = v.tensor_scalar(w8[:, c, :], w8[:, c, :], wsum[:, c, 1:2], ROUTED_SCALE, ALU.mult, ALU.mult)
                step(ins)
                for c in range(TC):
                    ins = v.tensor_copy(wgtt[:, c, 0:NOBLK].rearrange("p (j e) -> p j e", j=NJ),
                                        w8[:, c, :].unsqueeze(1).broadcast_to([P, NJ, NE]))
                step(ins)
                for c in range(TC):
                    dve.wait_ge(S("shared_silu"), 2 * L + c + 1)
                    hid = (sg, hh)[c]
                    v.tensor_tensor(hid, hid, PS[:, 5 + c, DE:2 * DE], ALU.mult).then_inc(S("shared_h"), 1)
                dve.wait_ge(S("rank_mm"), 1 * L + 1)
                for j in range(1, NJ):
                    ins = v.tensor_scalar(ovr[:, 0, (j - 1) * NE:j * NE], PS[:, 7, TC * NE:TC * NE + NE],
                                          CAP * j + 0.5, None, ALU.is_gt)
                step(v.scalar_tensor_tensor(mrep, PS[:, 7, 0:TC * NE].rearrange("p (c e) -> p c e", c=TC), AWAY, selm,
                                            ALU.add, ALU.mult))
                for j in range(NJ):
                    v.tensor_scalar(rankt[:, :, j * NE:(j + 1) * NE], mrep, -AWAY - CAP * j, None, ALU.add)
                step(v.tensor_tensor_scan(ovr[:, 1, :], onesr[:, :], ovr[:, 0, :], 0.0, ALU.mult, ALU.add))
                step(v.scalar_tensor_tensor(ovr[:, 2, :], ovr[:, 1, :], cst[:, C_S1:C_S1 + 1], ovr[:, 0, :],
                                            ALU.is_equal, ALU.mult))
                step(v.scalar_tensor_tensor(ovr[:, 2, :], ovr[:, 2, :], 1.0, cst[:, C_QM:C_QM + (NJ - 1) * NE],
                                            ALU.mult, ALU.mult, accum_out=ovs[:, 0:1]))
                v.tensor_scalar(cm[:, 0, 0:8], cst[:, C_KK:C_KK + 8], ovr[:, 1, (NJ - 1) * NE - 1:(NJ - 1) * NE], None,
                                ALU.is_lt).then_inc(S("over"), 1)
                dve.wait_ge(S("over"), 1 * L + 1)
                step(v.tensor_reduce(ovs[:, 1:2], cm[:, 0, 0:8], AX_X, ALU.add))
                v.tensor_scalar(tab[0:1, L, 0, TABLE - 1:TABLE], ovs[0:1, 1:2], float(NITER_MIN), None, ALU.add)
                v.tensor_scalar(tab[0:1, L, 0, TABLE - 2:TABLE - 1], ovs[0:1, 1:2], float(NITER_MIN - 1), None, ALU.add)
                dve.wait_ge(S("shared_t_mm"), 2 * L + TC)
                v.tensor_copy(shT.rearrange("p f c s -> p (f c s)"), PS[:, 4, :]).then_inc(S("shared_t_out"), 1)
                dve.wait_ge(S("over_mm"), 1 * L + 1)
                step(v.tensor_scalar(tab[0:1, L, 0, NE:NE + OVER], PS[0:1, 7, 256:256 + OVER], float(NOBLK), None, ALU.add))
                v.tensor_scalar(tab[0:1, L, 1, NE:NE + OVER], tab[0:1, L, 0, NE:NE + OVER], NE - 1, None,
                                ALU.bitwise_and).then_inc(S("table"), 1)

                def onehot(cols):
                    for s in range(4):
                        for c in range(TC):
                            ins = v.tensor_scalar(oh[:, c, s * CAP:s * CAP + CAP], iota, rankt[:, c, bass.ds(cols[s], 1)],
                                                  None, ALU.is_equal)
                    ins.then_inc(S(f"onehot_{L}"), 1)

                onehot(range(4))
                dve.sem_inc(S(f"hidden_{L}"), 1)
                dve.wait_ge(S("table"), 1 * L + 1)
                n = dve.value_load(tab[0:1, L, 0, TABLE - 1:TABLE], min_val=NITER_MIN, max_val=NITER_MAX)

                def column(at):
                    return dve.value_load(tab[0:1, L, 0, bass.ds(at, 1)], min_val=0, max_val=NOBLK)

                with dve.Fori(0, n) as i:
                    for b in range(2):
                        g = i * 2 + b
                        if b == 0:
                            cols = [column(i * 4 + (4 + s)) for s in range(4)]
                            dve.wait_ge(S(f"gather_mm_{L}"), i * 4 + 4)
                            onehot(cols)
                        cols = [column(i * 4 + (2 * b + s)) for s in range(2)]
                        dve.wait_ge(S(f"turn_mm_{L}"), g + 1)
                        for s in range(2):
                            for c in range(TC):
                                v.tensor_scalar(ohw[:, c, s * CAP:s * CAP + CAP], iota, rankt[:, c, bass.ds(cols[s], 1)],
                                                wgtt[:, c, bass.ds(cols[s], 1)], ALU.is_equal, ALU.mult)
                        dve.wait_ge(S(f"silu_{L}"), g + 1)
                        v.tensor_tensor(hh, sg, PS[:, 6, DE:2 * DE], ALU.mult).then_inc(S(f"hidden_{L}"), 1)
                        dve.wait_ge(S(f"turn_mm_{L}"), g + 2)
                        v.tensor_copy(hT.rearrange("p f s -> p (f s)"), PS[:, 7, 0:DE]).then_inc(S(f"hidT_{L}"), 1)
                        v.tensor_reduce(wslot[:, 0:1], PS[:, 7, DE:DE + T], AX_X, ALU.max)
                        v.tensor_scalar(ohT[:, :], PS[:, 7, DE:DE + T], 0.0, None, ALU.is_gt
                                        ).then_inc(S(f"turned_{L}"), 1)
                        for h in range(2):
                            hs = slice(h * HALF, h * HALF + HALF)
                            dve.wait_ge(S(f"y_hi_{L}"), g * 2 + h + 1)
                            v.scalar_tensor_tensor(y_lo[:, hs], PS[:, 4 + h, :], wslot[:, 0:1], y_hi[:, hs].bitcast(F32),
                                                   ALU.mult, ALU.subtract).then_inc(S(f"y_out_{L}"), 1)
                return n

            def ple(L, n):
                norm2(L, n)
                odd_banks(xT, "xT", 3 * L + 1)
                for t in range(TC * 2):
                    c, hs = t // 2, slice((t % 2) * HALF, (t % 2) * HALF + HALF)
                    dve.wait_ge(S("pgate"), 4 * L + t + 1)
                    step(v.tensor_tensor(z[:, c, hs], z[:, c, hs], PS[:, t, :], ALU.mult))
                    v.tensor_tensor(x_res[:, c, hs], x_res[:, c, hs], z[:, c, hs], ALU.add).then_inc(S("x_out"), 1)

            def norm2(L, n):
                dve.wait_ge(S(f"scatter_mm_{L}"), n * 2 + 1)
                for c in range(TC):
                    for h in range(2):
                        ins = residual(c, h)
                ins.then_inc(S("moe_read"), 1)
                dve.wait_ge(S("moe_read"), L + 1)
                for c in range(TC):
                    norm_stats(c, z)
                for c in range(TC):
                    norm_scale(3 * L + 1, c)
                norm_gain(3 * L + 1, 2 * L + 1, "x2_out")

            dve.wait_ge(x_in, 16)
            n = moe(0)
            ple(0, n)

            dve.wait_ge(S("x_out"), TC * 2)
            for c in range(TC):
                norm_stats(c, x_res)
            for c in range(TC):
                norm_scale(KV_NORM, c)
            odd_banks(xT, "xT", 2)

            def rope(copied, done):
                for t in range(TC * 2):
                    c, hs = t // 2, slice((t % 2) * HALF, (t % 2) * HALF + HALF)
                    src = PS[:, 4 + t, :].rearrange("p (h d) -> p h d", d=DH)
                    dst = tokm[:, c, hs].rearrange("p (h d) -> p h d", d=DH)
                    tb = cst[:, C_ROPE + c * 2 * ROT:C_ROPE + (c + 1) * 2 * ROT]
                    cc = tb[:, 0:ROT].unsqueeze(1).broadcast_to([P, 4, ROT])
                    s_neg = tb[:, ROT:ROT + HR].unsqueeze(1).broadcast_to([P, 4, HR])
                    s_pos = tb[:, ROT + HR:2 * ROT].unsqueeze(1).broadcast_to([P, 4, HR])
                    if t:
                        dve.wait_ge(S(done), t)
                    dve.wait_ge(S(copied), t + 1)
                    v.tensor_tensor(ropet[:, 0], src[:, :, 0:ROT], cc, ALU.mult)
                    v.tensor_tensor(ropet[:, 1, :, 0:HR], src[:, :, HR:ROT], s_neg, ALU.mult)
                    step(v.tensor_tensor(ropet[:, 1, :, HR:ROT], src[:, :, 0:HR], s_pos, ALU.mult))
                    v.tensor_tensor(dst[:, :, 0:ROT], ropet[:, 0], ropet[:, 1], ALU.add).then_inc(S(done), 1)

            rope("k_copied", "k_rope")
            odd_banks(kT, "heads", 0, 0)
            rope("q_copied", "q_rope")
            odd_banks(qT, "heads", 1, 0)

            def probs(h):
                dve.wait_ge(S("exped"), h + 1)
                step(v.reciprocal(mxs[:, h, :, 3], mxs[:, h, :, 2]))
                v.tensor_scalar(prob[:, h % 2, 0:P], prob[:, h % 2, 0:P], mxs[:, h, 0, 3:4], None, ALU.mult)
                v.tensor_scalar(prob[:, h % 2, P:3 * P], prob[:, h % 2, P:3 * P], mxs[:, h, 1, 3:4], None, ALU.mult
                                ).then_inc(S("probs"), 1)

            for i in range(NH + 1):
                if i < NH:
                    dve.wait_ge(S("score_mm"), i + 1)
                    v.tensor_reduce(mxs[:, i, 0, 0:1], PS[:, 4 + i % 2, 0:P], AX_X, ALU.max)
                    step(v.tensor_reduce(mxs[:, i, 1, 0:1], PS[:, 4 + i % 2, P:3 * P], AX_X, ALU.max))
                    v.tensor_scalar(mxs[:, i, :, 1], mxs[:, i, :, 0], -SCALE, None, ALU.mult).then_inc(S("negmax"), 1)
                if i >= 1:
                    probs(i - 1)
            n = moe(1)
            ple(1, n)


def constants():
    c = np.zeros((P, C_N), np.float32)
    p = np.arange(P)
    c[:, C_ID:C_ID + P] = np.eye(P)
    c[:, C_IOTA:C_IOTA + CAP] = np.arange(CAP)
    inv = np.float32(500000.0) ** (-np.arange(0, ROT, 2, dtype=np.float32) / np.float32(ROT))
    ang = np.arange(T, dtype=np.float32)[:, None] * inv[None, :]
    cos, sin = np.cos(ang), np.sin(ang)
    rope = np.concatenate([cos, cos, -sin, sin], axis=1).reshape(TC, P, 2 * ROT).transpose(1, 0, 2)
    c[:, C_ROPE:C_ROPE + TC * 2 * ROT] = rope.reshape(P, -1)
    c[:, C_QM:C_QM + (NJ - 1) * NE] = np.arange(NE, NJ * NE) - NOBLK
    g = np.arange(NG)
    c[:, C_LT:C_LT + NG * NG] = (g[None, :] < g[:, None]).reshape(-1)
    c[:, C_KK:C_KK + 8] = 4 * np.arange(8)
    c[:, C_S1] = 1 + p
    t = np.full((1, LAYERS, 2, TABLE), NOBLK, np.int32)
    t[:, :, 1, :] = 0
    t[:, :, :, 0:NE] = np.arange(NE)
    b = np.stack([np.eye(P), p[:, None] < p[None, :], np.ones((P, P)), np.where(p[None, :] <= p[:, None], 0.0, -1e30)], axis=1)
    return c, b.astype(np.dtype("bfloat16")), t


def kernel(x, p, ln_g, ln_b, a_w_in, a_b_in, a_conv_w, a_conv_b, a_gate_a_w, a_gate_a_b, a_gate_i_w,
           a_gate_i_b, a_lambda, a_w_out, kv_ln_g, kv_ln_b, w_kv, b_w_q, b_w_o, router_w, router_b,
           exp_w_gate, exp_w_up, exp_w_down, sh_w_gate, sh_w_up, sh_w_down, ple_w, ple_gate_w):
    import concourse.bacc as bacc
    from concourse.bass_utils import run_bass_kernel_spmd

    def chunks(w):
        w = np.asarray(w)
        return w.reshape(-1, P, w.shape[-1]).transpose(1, 0, 2)

    def units(w):
        return chunks(w).reshape(P, -1, UNIT).transpose(1, 0, 2)

    def channels(*vs):
        return np.concatenate([np.asarray(v).reshape(-1, P).T for v in vs], axis=1)

    def tokens(a):
        return chunks(a)

    x = np.asarray(x)
    win = np.asarray(a_w_in)[0].reshape(KC, P, 2 * KC, P).transpose(1, 2, 0, 3)
    gates = [np.asarray(w)[0].reshape(4, 2, P, 2 * P).transpose(2, 0, 1, 3).reshape(P, UNIT)
             for w in (a_gate_a_w, a_gate_i_w)]
    wg, wu, wd = (np.asarray(w) for w in (exp_w_gate, exp_w_up, exp_w_down))
    experts = np.empty((LAYERS, NE, P, EXPERT), np.float32)
    gu = experts[..., :GU].reshape(LAYERS, NE, P, KC, 2, DE)
    gu[..., 0, :] = wg.reshape(LAYERS, NE, KC, P, DE).transpose(0, 1, 3, 2, 4)
    gu[..., 1, :] = wu.reshape(LAYERS, NE, KC, P, DE).transpose(0, 1, 3, 2, 4)
    experts[..., GU:].reshape(LAYERS, NE, P, FC, D)[...] = wd.reshape(LAYERS, NE, FC, P, D).transpose(0, 1, 3, 2, 4)
    shared = np.stack([np.concatenate([
        np.stack([chunks(np.asarray(sh_w_gate)[i]), chunks(np.asarray(sh_w_up)[i])], axis=2).reshape(P, GU),
        chunks(np.asarray(sh_w_down)[i]).reshape(P, UNIT)], axis=1) for i in range(LAYERS)])
    kv = np.asarray(w_kv)
    lg, lb = np.asarray(ln_g), np.asarray(ln_b)
    rows = np.concatenate([np.stack([lg, lb], axis=2).reshape(-1), np.asarray(router_b).reshape(-1)])
    cst, cstb, tab = constants()
    feeds = {
        "xt": tokens(x[0].T), "x": chunks(x[0]), "pt": np.stack([tokens(np.asarray(p)[i, 0].T) for i in range(LAYERS)], axis=1),
        "cst": cst, "cstb": cstb,
        "chan": channels(np.asarray(a_b_in)[0], np.asarray(a_conv_w)[0], np.asarray(a_conv_b)[0], np.asarray(a_gate_a_b)[0],
                         np.asarray(a_gate_i_b)[0], np.asarray(a_lambda)[0], kv_ln_g, kv_ln_b),
        "rows": rows, "tab": tab, "win": win.reshape(P, KC, UNIT).transpose(1, 0, 2), "gates": np.stack(gates),
        "wout": units(np.asarray(a_w_out)[0]),
        "shared": shared.reshape(LAYERS, P, 3, UNIT).transpose(0, 2, 1, 3),
        "router": chunks(np.concatenate([np.asarray(router_w)[i] for i in range(LAYERS)], axis=1)),
        "experts": experts, "ple": np.concatenate([units(np.asarray(ple_w)[i]) for i in range(LAYERS)]),
        "pgate": np.stack([units(np.asarray(ple_gate_w)[i]) for i in range(LAYERS)]),
        "wkv": np.stack([units(kv[:, :D]), units(kv[:, D:])]), "wq": units(np.asarray(b_w_q)[0]),
        "wo": units(np.asarray(b_w_o)[0]),
    }
    nc = bacc.Bacc("TRN2", target_bir_lowering=False, num_devices=1, dynamic_dma_scratch_size=1024)
    arrays, args = {}, []
    for name, v in feeds.items():
        v = np.ascontiguousarray(v)
        arrays[f"in_{name}"] = v
        args.append(nc.dram_tensor(f"in_{name}", v.shape, mybir.dt.from_np(v.dtype), kind="ExternalInput").ap())
    args.append(nc.dram_tensor("out", (1, T, D), F32, kind="ExternalOutput").ap())
    build(nc, *args)
    r = run_bass_kernel_spmd(nc, [arrays], core_ids=[0])
    return r.results[0]["out"]
```
